# Optimizing a Trainium2 kernel written in Bass

```python
import jax, jax.numpy as jnp
from jax import lax
import numpy as np

D_MODEL = 2048
BATCH = 1
SEQ = 512
DEPTH = 1

SGU_WIDTH = D_MODEL
SGU_GROUPS = 8
SGU_GROUP_DIM = SGU_WIDTH // SGU_GROUPS
SGU_CHUNK = 128
GLA_HEADS = 4
GLA_KEY_WIDTH = D_MODEL // 2
GLA_VALUE_WIDTH = D_MODEL
GLA_HEAD_K = GLA_KEY_WIDTH // GLA_HEADS
GLA_HEAD_V = GLA_VALUE_WIDTH // GLA_HEADS
GLA_GATE_RANK = 16
GLA_GATE_TEMP = 16.0
GLA_CHUNK = 64
PEER_HEADS = 8
PEER_N_KEYS = 128
PEER_N_EXPERTS = PEER_N_KEYS * PEER_N_KEYS
PEER_QUERY_DIM = 256
PEER_HALF = PEER_QUERY_DIM // 2
PEER_TOPK = 16
PEER_TOKEN_BLOCK = 64
EPS = 1e-6

IN_SPLIT_SIZES = (SGU_WIDTH, SGU_WIDTH,
                  GLA_KEY_WIDTH, GLA_KEY_WIDTH,
                  GLA_VALUE_WIDTH, GLA_VALUE_WIDTH,
                  GLA_GATE_RANK,
                  D_MODEL, D_MODEL)
IN_WIDTH = sum(IN_SPLIT_SIZES)

kernel_name = "hybrid_sgu_gla_peer_block"

def rmsnorm(x, g):
    xf = x.astype(jnp.float32)
    y = xf * lax.rsqrt(jnp.mean(xf * xf, axis=-1, keepdims=True) + EPS)
    return (y * g.astype(jnp.float32)).astype(x.dtype)

def layernorm(x, g, b):
    xf = x.astype(jnp.float32)
    mu = jnp.mean(xf, axis=-1, keepdims=True)
    var = jnp.mean(jnp.square(xf - mu), axis=-1, keepdims=True)
    y = (xf - mu) * lax.rsqrt(var + EPS)
    return (y * g.astype(jnp.float32) + b.astype(jnp.float32)).astype(x.dtype)

def split_columns(p):
    offsets = []
    acc = 0
    for s in IN_SPLIT_SIZES[:-1]:
        acc += s
        offsets.append(acc)
    return jnp.split(p, offsets, axis=-1)

def spatial_gating(u, v, w_s, b_s, ln_g, ln_b):
    B, S, _ = v.shape
    n = S // SGU_CHUNK
    v = layernorm(v, ln_g, ln_b).reshape(B, n, SGU_CHUNK, SGU_GROUPS, SGU_GROUP_DIM)
    causal = jnp.tril(jnp.ones((SGU_CHUNK, SGU_CHUNK), dtype=bool))
    w = jnp.where(causal[None], w_s, 0.0)
    s = jnp.einsum('gts,bnsgc->bntgc', w, v) + b_s.T[None, None, :, :, None]
    return u * s.reshape(B, S, SGU_WIDTH)

def gla_chunked(q, k, v, log_a):
    B, S, H, dk = q.shape
    dv = v.shape[-1]
    n = S // GLA_CHUNK

    def to_chunks(t):
        return t.astype(jnp.float32).reshape(B, n, GLA_CHUNK, H, t.shape[-1]).transpose(0, 3, 1, 2, 4)

    q = to_chunks(q) * (dk ** -0.5)
    k = to_chunks(k)
    v = to_chunks(v)
    b = jnp.cumsum(to_chunks(log_a), axis=-2)
    q_dec = q * jnp.exp(b)
    k_inv = k * jnp.exp(-b)
    causal = jnp.tril(jnp.ones((GLA_CHUNK, GLA_CHUNK), dtype=bool))
    att = jnp.where(causal, jnp.einsum('bhncd,bhnsd->bhncs', q_dec, k_inv), 0.0)
    o_intra = jnp.einsum('bhncs,bhnse->bhnce', att, v)
    b_last = b[..., -1, :]
    k_end = k * jnp.exp(b_last[..., None, :] - b)

    def step(state, inp):
        qc, kc, vc, dc = inp
        o = jnp.einsum('bhcd,bhde->bhce', qc, state)
        state = state * dc[..., None] + jnp.einsum('bhcd,bhce->bhde', kc, vc)
        return state, o

    xs = (jnp.moveaxis(q_dec, 2, 0), jnp.moveaxis(k_end, 2, 0),
          jnp.moveaxis(v, 2, 0), jnp.moveaxis(jnp.exp(b_last), 2, 0))
    _, o_inter = lax.scan(step, jnp.zeros((B, H, dk, dv), jnp.float32), xs)
    o = o_intra + jnp.moveaxis(o_inter, 0, 2)
    return o.transpose(0, 2, 3, 1, 4).reshape(B, S, H, dv)

def gla_branch(q, k, v, r, a_low, w_alpha_up, b_alpha, norm_g):
    B, S, _ = q.shape
    log_a = jax.nn.log_sigmoid((a_low @ w_alpha_up + b_alpha).astype(jnp.float32)) / GLA_GATE_TEMP
    o = gla_chunked(q.reshape(B, S, GLA_HEADS, GLA_HEAD_K),
                    k.reshape(B, S, GLA_HEADS, GLA_HEAD_K),
                    v.reshape(B, S, GLA_HEADS, GLA_HEAD_V),
                    log_a.reshape(B, S, GLA_HEADS, GLA_HEAD_K))
    o = rmsnorm(o, norm_g) * jax.nn.silu(r.astype(jnp.float32)).reshape(B, S, GLA_HEADS, GLA_HEAD_V)
    return o.reshape(B, S, GLA_VALUE_WIDTH).astype(q.dtype)

def peer(h, w_query, sub_keys, expert_u, expert_v):
    B, S, D = h.shape
    T = B * S
    hf = h.reshape(T, D)
    q = (hf @ w_query).reshape(T, PEER_HEADS, 2, PEER_HALF)
    s = jnp.einsum('thpd,hpkd->thpk', q, sub_keys).astype(jnp.float32)
    s1, i1 = lax.top_k(s[:, :, 0], PEER_TOPK)
    s2, i2 = lax.top_k(s[:, :, 1], PEER_TOPK)
    cand = (s1[..., :, None] + s2[..., None, :]).reshape(T, PEER_HEADS, PEER_TOPK * PEER_TOPK)
    cand_idx = (i1[..., :, None] * PEER_N_KEYS + i2[..., None, :]).reshape(T, PEER_HEADS, PEER_TOPK * PEER_TOPK)
    best, pos = lax.top_k(cand, PEER_TOPK)
    idx = jnp.take_along_axis(cand_idx, pos, axis=-1)
    gate = jax.nn.softmax(best, axis=-1).astype(h.dtype)

    nb = T // PEER_TOKEN_BLOCK

    def block(args):
        hb, ib, gb = args
        u = jnp.take(expert_u, ib, axis=0)
        act = jnp.einsum('td,thkd->thk', hb, u)
        wgt = gb * jax.nn.gelu(act, approximate=False)
        vv = jnp.take(expert_v, ib, axis=0)
        return jnp.einsum('thk,thkd->td', wgt, vv)

    out = lax.map(block, (hf.reshape(nb, PEER_TOKEN_BLOCK, D),
                          idx.reshape(nb, PEER_TOKEN_BLOCK, PEER_HEADS, PEER_TOPK),
                          gate.reshape(nb, PEER_TOKEN_BLOCK, PEER_HEADS, PEER_TOPK)))
    return out.reshape(B, S, D)

def setup_inputs(seed: int = 0) -> dict:
    key = jax.random.key(seed)
    ks = jax.random.split(key, 20)
    f32 = jnp.float32
    L, D = DEPTH, D_MODEL

    def nrm(k, shape, scale):
        return jax.random.normal(k, shape, f32) * scale

    return {
        "x": jax.random.normal(ks[0], (BATCH, SEQ, D), f32),
        "g_mix": 1.0 + nrm(ks[1], (L, D), 0.02),
        "w_in": nrm(ks[2], (L, D, IN_WIDTH), D ** -0.5),
        "w_s": nrm(ks[3], (L, SGU_GROUPS, SGU_CHUNK, SGU_CHUNK), SGU_CHUNK ** -0.5),
        "b_s": 1.0 + nrm(ks[4], (L, SGU_GROUPS, SGU_CHUNK), 0.02),
        "ln_v_g": 1.0 + nrm(ks[5], (L, SGU_WIDTH), 0.02),
        "ln_v_b": nrm(ks[6], (L, SGU_WIDTH), 0.02),
        "w_alpha_up": nrm(ks[7], (L, GLA_GATE_RANK, GLA_KEY_WIDTH), GLA_GATE_RANK ** -0.5),
        "b_alpha": nrm(ks[8], (L, GLA_KEY_WIDTH), 0.02),
        "gla_norm_g": 1.0 + nrm(ks[9], (L, GLA_HEAD_V), 0.02),
        "w_branch_a": nrm(ks[10], (L, SGU_WIDTH, D), SGU_WIDTH ** -0.5),
        "w_branch_b": nrm(ks[11], (L, GLA_VALUE_WIDTH, D), GLA_VALUE_WIDTH ** -0.5),
        "w_out": nrm(ks[12], (L, D, D), D ** -0.5),
        "g_ffn": 1.0 + nrm(ks[13], (L, D), 0.02),
        "w_query": nrm(ks[14], (L, D, PEER_HEADS * PEER_QUERY_DIM), D ** -0.5),
        "sub_keys": nrm(ks[15], (L, PEER_HEADS, 2, PEER_N_KEYS, PEER_HALF), PEER_HALF ** -0.5),
        "expert_u": nrm(ks[16], (L, PEER_N_EXPERTS, D), D ** -0.5),
        "expert_v": nrm(ks[17], (L, PEER_N_EXPERTS, D), D ** -0.5),
        "g_final": 1.0 + nrm(ks[18], (D,), 0.02),
    }

def reference(x, g_mix, w_in, w_s, b_s, ln_v_g, ln_v_b, w_alpha_up, b_alpha, gla_norm_g,
              w_branch_a, w_branch_b, w_out, g_ffn, w_query, sub_keys, expert_u, expert_v, g_final):
    for l in range(DEPTH):
        h = rmsnorm(x, g_mix[l])
        a_u, a_v, b_q, b_k, b_v, b_r, b_alow, gate_a, gate_b = split_columns(h @ w_in[l])
        y_a = spatial_gating(jax.nn.gelu(a_u, approximate=False), jax.nn.gelu(a_v, approximate=False),
                             w_s[l], b_s[l], ln_v_g[l], ln_v_b[l]) @ w_branch_a[l]
        y_b = gla_branch(b_q, b_k, b_v, b_r, b_alow, w_alpha_up[l], b_alpha[l], gla_norm_g[l]) @ w_branch_b[l]
        merged = jax.nn.sigmoid(gate_a) * y_a + jax.nn.sigmoid(gate_b) * y_b
        x = x + merged @ w_out[l]
        h2 = rmsnorm(x, g_ffn[l])
        x = x + peer(h2, w_query[l], sub_keys[l], expert_u[l], expert_v[l])
    return rmsnorm(x, g_final)


_drawn_inputs = setup_inputs


def setup_inputs(seed=0):
    import zlib

    import numpy as np

    out = dict(_drawn_inputs(seed))
    spreads = {}
    factors = {'g_mix': 3.481,
     'b_s': 8.0,
     'ln_v_g': 8.0,
     'ln_v_b': 8.0,
     'b_alpha': 8.0,
     'gla_norm_g': 8.0,
     'g_ffn': 8.0,
     'w_query': 6.018,
     'sub_keys': 6.024,
     'expert_u': 6.629,
     'expert_v': 5.993,
     'g_final': 2.841}
    for name, (base, spread) in spreads.items():
        noise = np.random.default_rng([zlib.crc32(name.encode()), seed]).standard_normal(out[name].shape)
        drawn = base * np.exp(spread * noise) if base else spread * noise
        out[name] = __import__('jax').numpy.asarray(drawn.astype(out[name].dtype))
    for name, factor in factors.items():
        out[name] = (out[name] * factor).astype(out[name].dtype)
    return out
```

```python
from contextlib import ExitStack, contextmanager

import concourse.bass as bass
from concourse import mybir

F32 = mybir.dt.float32
F32R = mybir.dt.float32r
U32 = mybir.dt.uint32
BF16 = mybir.dt.bfloat16
ALU = mybir.AluOpType
ACT = mybir.ActivationFunctionType
AX_X = mybir.AxisListType.X

P = 128
T = 512
D = 2048
TT = T // P
KT = D // P
BW = 512
NB = D // BW
HEADS = 4
DK, DV = 256, 512
DT = DK // P
CHUNK = 64
NCH = T // CHUNK
GROUPS = 8
RANK = 16
PH = 8
KEYS = 128
TOPK = 16
ETILES = 128
EG = 4
EPS = 1e-6
GATE_TEMP = 16.0
LOWEST = -3.4e38
WTOK = 8
STAGE_TOK = 64

LEAD = 16
STAGE_UNITS = (ETILES - LEAD) // (T // STAGE_TOK)
PIECES = 4
N_CONST = 8
N_UNITS = 1 + KT + 2 * KT + KT + HEADS * (2 * 2 + 4 + 4) + 4 * KT + ETILES + ETILES


class Count:

    def __init__(self, start=0):
        self.base, self.k, self.total = start, 0, 0

    def next(self, by=1):
        self.k += by
        self.total += by
        return self.base + self.k

    def now(self, off=0):
        return self.base + (self.k + off)


def positions():
    unit, acc, evac, found = 0, 0, [1] * 4, {}
    for name, units, accs, reads in (
            ("alow", 1, 0, (1, 0, 0, 0)), ("v", KT, 3 * NB, (NB,) * 4), ("gates", 2 * KT, 0, (KT, KT, 0, 0)),
            ("spatial", KT, 0, (KT // 2, KT // 2, 0, 0)),
            ("attention", 12 * HEADS, 6 * HEADS, (3 * HEADS,) * 4),
            ("merge_spatial", KT, 0, (KT // 2, KT // 2, 0, 0)),
            ("merge_attention", KT, 0, (KT // 2, KT // 2, 0, 0)),
            ("residual", KT, 3 * NB, (NB,) * 4), ("query", KT, 0, (KT // 2, KT // 2, 0, 0)),
            ("experts", ETILES, 0, (ETILES // 2, ETILES // 2, 0, 0)),
            ("values", ETILES, 3 * ETILES, (ETILES,) * 4), ("end", 0, 0, (0,) * 4)):
        found[name] = {"unit": unit, "acc": acc, "evac": list(evac)}
        unit, acc, evac = unit + units, acc + accs, [e + r for e, r in zip(evac, reads)]
    assert unit == N_UNITS
    return found


AT = positions()


@contextmanager
def repeat(eng, n, *counts):
    with eng.Fori(0, n) as i:
        starts = [(c.base, c.k, c.total) for c, _ in counts]
        for c, per in counts:
            c.base, c.k = i * per + (c.base + c.k), 0
        yield i
        for (c, per), (_, _, total) in zip(counts, starts):
            assert c.total - total == per, (c.total - total, per)
    for (c, per), (base, k, total) in zip(counts, starts):
        c.base, c.k, c.total = base + (k + n * per), 0, total + n * per


def program(nc, x, weights, g_mix, g_ffn, g_final, w_s_t, b_s, ln_g, ln_b, w_up, b_alpha, norm_g,
            keys_t, out):
    with ExitStack() as ctx:
        place = [nc.sbuf_base + 31 & ~31]

        def at(name, shape, dtype, offset):
            return nc.alloc_sbuf_tensor_at(name, shape, dtype, offset=offset)

        def room(kilobytes):
            start = place[0]
            place[0] += int(kilobytes * 1024)
            return start

        x_high = at("x_high", [P, KT, T], F32R, room(32))
        x_low = at("x_low", [P, KT, T], F32R, room(32))
        raw = at("raw", [P, 2, D], F32, room(16))
        high = at("high", [P, 2, D], F32R, room(16))
        low = at("low", [P, 2, D], F32R, room(16))
        region_a = room(32)
        xa = at("xa", [P, TT, D], F32, region_a)
        region_b = room(32)
        xb = at("xb", [P, TT, D], F32, region_b)
        small = room(2.15625)
        region_c = room(0)
        end = nc.sbuf_top

        class Region:
            def __init__(self, start, limit):
                self.at, self.limit = start, limit

            def __call__(self, name, shape, dtype=F32):
                n = 2 if dtype == BF16 else 4
                for s in shape[1:]:
                    n *= s
                t = at(name, shape, dtype, self.at)
                self.at += n + 31 & ~31
                assert self.at <= self.limit, (name, self.at, self.limit)
                return t

        c = Region(small, region_c)
        ident = c("ident", [P, P])
        iota = c("iota", [P, KEYS])
        iota16 = c("iota16", [P, TOPK])
        gmix = c("gmix", [P, KT])
        gffn = c("gffn", [P, KT])
        normg = c("normg", [P, DV // P])
        balpha = c("balpha", [P, HEADS * DT])
        squares = c("squares", [P, 2, TT])
        squares_sum = c("squares_sum", [P, TT])
        norm_ms = c("norm_ms", [P, TT])
        norm_root = c("norm_root", [P, TT])
        norm_inv = c("norm_inv", [P, TT])
        wait_at = c("wait_at", [P, 1])
        head_squares = c("head_squares", [P, TT])
        head_ms = c("head_ms", [P, TT])
        head_root = c("head_root", [P, TT])
        head_inv = c("head_inv", [P, TT])
        var = c("var", [P, TT])
        var_root = c("var_root", [P, TT])
        var_inv = c("var_inv", [P, TT])
        bn = c("bn", [P, TT, NB, 6])
        mean_var = c("mean_var", [P, TT, 2])

        c = Region(region_c, end)
        alow_t = c("alow_t", [P, T])
        scan_keep = c("scan_keep", [P, T])
        att_keep = c("att_keep", [P, P])
        kept = c.at
        lng = c("lng", [P, D])
        lnb = c("lnb", [P, D])
        bs = c("bs", [P, GROUPS, P])
        ws = c("ws", [P, GROUPS, P])
        vstage = c("vstage", [P, TT, 2 * P])
        ws_stage = c("ws_stage", [P, P])
        sgu_act = c("sgu_act", [P, 2, T])
        sgu_sum = c("sgu_sum", [P, T])
        c = Region(kept, end)
        k_inv = c("k_inv", [P, DT, T])
        k_end = c("k_end", [P, DT, T])
        q_dec = c("q_dec", [P, DT, T])
        q_in = c("q_in", [P, DT, T])
        vals = c("vals", [P, TT, DV])
        k_end_t = c("k_end_t", [P, TT, DK])
        att_t = c("att_t", [P, TT, P])
        state = c("state", [P, DT, DV])
        decay = c("decay", [P, DT, NCH])
        k_decay = c("k_decay", [P, DT, NCH])
        q_decay = c("q_decay", [P, DT, NCH])
        wup_stage = c("wup_stage", [P, DK])
        silu_out = c("silu_out", [P, 2, DV])
        c = Region(region_c, end)
        merged = c("merged", [P, KT, T])
        gate_in = c("gate_in", [P, 2, T])
        gate_mul = c("gate_mul", [P, T])
        c = Region(region_c, end)
        skeys = c("skeys", [P, 2 * PH, KEYS])
        q_t = c("q_t", [P, 2, T])
        scores = c("scores", [P, 2, T])
        masked = c("masked", [P, TT, KEYS])
        top_v = c("top_v", [P, TT, 2, TOPK])
        top_i = c("top_i", [P, TT, 2, TOPK], U32)
        cand = c("cand", [P, TT, TOPK * TOPK])
        cand_masked = c("cand_masked", [P, TT, TOPK * TOPK])
        best = c("best", [P, TT, TOPK])
        pos = c("pos", [P, TT, TOPK], U32)
        all_i = c("all_i", [P, TT, 2, PH, TOPK])
        all_best = c("all_best", [P, TT, PH, TOPK])
        all_pos = c("all_pos", [P, TT, PH, TOPK], U32)
        peer_sum = c("peer_sum", [P, 2, TT * PH])
        act_out = at("act_out", [P, 2, T], F32, end - 4096)
        assert c.at <= end - 4096
        c = Region(region_b, region_b + 32 * 1024)
        pos_half = c("pos_half", [P, 2, TT, P], U32)
        pos_f = c("pos_f", [P, 2, TT, P])
        expert_i = c("expert_i", [P, 2, TT, P])
        onehot16 = c("onehot16", [P, P, TOPK])
        picked = c("picked", [P, P, TOPK])
        c = Region(region_c, end - 4096)
        idx1_t = c("idx1_t", [P, T])
        idx2_t = c("idx2_t", [P, T])
        gate_rest = c("gate_rest", [P, T])
        gate_rest2 = c("gate_rest2", [P, T])
        gate_parts = c("gate_parts", [P, 3, T], BF16)
        hit1 = c("hit1", [P, WTOK, P], BF16)
        rows = c("rows", [P, 3, WTOK, P], BF16)
        hit2 = c("hit2", [P, WTOK, P], BF16)
        assert c.at <= region_c + 24 * 1024
        stage = at("stage", [P, P, STAGE_TOK], F32, region_b)
        act_in = at("act_in", [P, 2, EG, T], F32, region_b)
        gates_in = at("gates_in", [P, 2, EG, T], F32, region_b + 16 * 1024)
        a_high = at("a_high", [P, 2, EG, T], F32R, region_c)
        a_low = at("a_low", [P, 2, EG, T], F32R, region_c + 16 * 1024)
        gfin = at("gfin", [P, D], F32, region_c + 32 * 1024)
        assert region_c + 40 * 1024 <= end - 4096

        bank = [ctx.enter_context(nc.psum_tensor(f"bank{b}", [P, BW], F32)) for b in range(8)]

        gates_dram = nc.dram_tensor("gates_dram", (2 * KT, P, T), F32).ap()
        act_dram = nc.dram_tensor("act_dram", (ETILES, P, T), F32).ap()
        retrieved_dram = nc.dram_tensor("retrieved_dram", (ETILES, P, T), F32).ap()

        def sem(name):
            return ctx.enter_context(nc.semaphore(name))

        raw_in = [sem("raw_in0"), sem("raw_in1")]
        high_done = sem("high_done")
        low_done = sem("low_done")
        unit_done = sem("unit_done")
        acc_done = sem("acc_done")
        evac = [sem(f"evac{b}") for b in range(4)]
        turned = sem("turned")
        xh_done = sem("xh_done")
        xl_done = sem("xl_done")
        x_in = [sem(f"x_in{t}") for t in range(TT)]
        const_in = sem("const_in")
        keys_in = sem("keys_in")
        gfin_in = sem("gfin_in")
        const_made = sem("const_made")
        sq_done = sem("sq_done")
        ms_done = sem("ms_done")
        root_done = sem("root_done")
        normed = sem("normed")
        dve_step = sem("dve_step")
        act_step = sem("act_step")
        pool_step = sem("pool_step")
        var_done = sem("var_done")
        var_rooted = sem("var_rooted")
        vstage_done = sem("vstage_done")
        mixed = sem("mixed")
        sgu_done = sem("sgu_done")
        gates_out = [sem("gates_out0"), sem("gates_out1")]
        wup_staged = sem("wup_staged")
        z_done = sem("z_done")
        soft_done = sem("soft_done")
        cum_done = sem("cum_done")
        exps_done = sem("exps_done")
        k_done = sem("k_done")
        q_done = sem("q_done")
        ke_turned = sem("ke_turned")
        ke_done = sem("ke_done")
        att_done = sem("att_done")
        att_kept = sem("att_kept")
        state_mm = sem("state_mm")
        state_done = sem("state_done")
        o_mm = sem("o_mm")
        o_done = sem("o_done")
        head_ms_done = sem("head_ms_done")
        head_rooted = sem("head_rooted")
        y_done = sem("y_done")
        gate_loaded = [sem("gate_loaded0"), sem("gate_loaded1")]
        merge_done = sem("merge_done")
        x_again = sem("x_again")
        scored = sem("scored")
        scores_done = sem("scores_done")
        topped = sem("topped")
        peer_diff = sem("peer_diff")
        peer_exp = sem("peer_exp")
        slots_done = sem("slots_done")
        slots_turned = sem("slots_turned")
        slot_gate_high = sem("slot_gate_high")
        rows_done = sem("rows_done")
        step_mm = sem("step_mm")
        step_out = sem("step_out")
        stage_out = sem("stage_out")
        act_stored = [sem("act_stored0"), sem("act_stored1")]
        pair_in = [sem("pair_in0"), sem("pair_in1")]
        product_done = sem("product_done")
        ah_done = sem("ah_done")
        al_done = sem("al_done")
        out_done = sem("out_done")

        block = ctx.enter_context(nc.Block())

        @block.sync
        def _(sp):
            for t in range(TT):
                sp.dma_start(xa[:, t, :], x[t * P:(t + 1) * P, :]).then_inc(x_in[t], 16)
            unit = Count()
            for u in range(3):
                n = unit.next()
                if u == 2:
                    sp.wait_ge(low_done, n - 2)
                sp.dma_start(raw[:, u % 2, :], weights[u]).then_inc(raw_in[u % 2], 16)
            with repeat(sp, (N_UNITS - 3) // 2, (unit, 2)) as i:
                for slot in (1, 0):
                    n = unit.next()
                    sp.wait_ge(low_done, n - 2)
                    src = weights[bass.ds(i * 2 + (4 - slot), 1)].rearrange("a p n -> (a p) n")
                    sp.dma_start(raw[:, slot, :], src).then_inc(raw_in[slot], 16)

        @block.gpsimd
        def _(pool):
            step = Count()

            def then(ins):
                ins.then_inc(pool_step, 1)
                pool.wait_ge(pool_step, step.next())

            nc.gpsimd.iota(iota[:], pattern=[[1, KEYS]], base=0, channel_multiplier=0,
                           allow_small_or_imprecise_dtypes=True)
            nc.gpsimd.iota(iota16[:], pattern=[[1, TOPK]], base=0, channel_multiplier=0,
                           allow_small_or_imprecise_dtypes=True)
            then(nc.gpsimd.memset(ident[:], 0.0))
            nc.gpsimd.affine_select(out=ident[:], in_=ident[:], compare_op=ALU.not_equal, fill=1.0, base=0,
                                    pattern=[[-1, P]], channel_multiplier=1).then_inc(const_made, 1)
            then(nc.gpsimd.memset(scan_keep[:], 1.0))
            nc.gpsimd.memset(scan_keep[:].rearrange("p (n c) -> p n c", c=CHUNK)[:, :, 0:1], 0.0)
            then(nc.gpsimd.memset(att_keep[:], 1.0))
            then(nc.gpsimd.affine_select(out=att_keep[:], in_=att_keep[:], compare_op=ALU.is_ge, fill=0.0,
                                         base=0, pattern=[[1, P]], channel_multiplier=-1))
            pool.wait_ge(const_in, 16 * N_CONST)
            nc.gpsimd.affine_select(out=ws[:], in_=ws[:], compare_op=ALU.is_ge, fill=0.0, base=0,
                                    pattern=[[0, GROUPS], [1, P]],
                                    channel_multiplier=-1).then_inc(const_made, 1)
            unit = Count()

            def low_part(slot):
                pool.wait_ge(high_done, unit.next())
                nc.gpsimd.tensor_tensor(low[:, slot, :], raw[:, slot, :], high[:, slot, :].bitcast(F32),
                                        ALU.subtract).then_inc(low_done, 1)

            low_part(0)
            with repeat(pool, (N_UNITS - 1) // 2, (unit, 2)):
                low_part(1)
                low_part(0)

        @block.scalar
        def _(act):
            step = Count()
            unit, slot = Count(), 0
            slot_in = [Count(), Count()]
            turns = Count()

            def then(ins):
                ins.then_inc(act_step, 1)
                act.wait_ge(act_step, step.next())

            def high_part(first=False):
                nonlocal slot
                n = unit.next()
                if not first:
                    act.wait_ge(unit_done, n - 2)
                act.wait_ge(raw_in[slot], slot_in[slot].next(16))
                nc.scalar.activation(high[:, slot, :], raw[:, slot, :], ACT.Copy).then_inc(high_done, 1)
                slot ^= 1

            def units(n):
                return [(unit, n), (slot_in[0], 8 * n), (slot_in[1], 8 * n)]

            def high_turned(gain):
                for k in range(KT):
                    act.wait_ge(turned, turns.next())
                    nc.scalar.activation(x_high[:, k, :], bank[4 + k % 4][:], ACT.Copy,
                                         scale=gain(k)).then_inc(xh_done, 1)

            def square_sum(t, part, start, stop):
                nc.scalar.activation(xb[:, t, start:stop], xa[:, t, start:stop], ACT.Square,
                                     accum_out=squares[:, part, t:t + 1]).then_inc(sq_done, 1)

            for b in range(4):
                act.sem_inc(evac[b], 1)
            act.sem_inc(step_out, 2)
            for dst, src in ((gmix[:], g_mix), (gffn[:], g_ffn), (normg[:], norm_g), (balpha[:], b_alpha),
                             (ws[:], w_s_t),
                             (lng[:], ln_g.partition_broadcast(P)), (lnb[:], ln_b.partition_broadcast(P)),
                             (bs[:].rearrange("p g t -> p (g t)"), b_s.partition_broadcast(P))):
                act.dma_start(dst, src).then_inc(const_in, 16)

            for t in range(TT):
                act.wait_ge(x_in[t], 16)
                square_sum(t, 0, 0, D - BW)
                square_sum(t, 1, D - BW, D)
            act.wait_ge(ms_done, 1)
            nc.scalar.activation(norm_root[:], norm_ms[:], ACT.Sqrt).then_inc(root_done, 1)
            high_part(first=True)
            high_part(first=True)
            act.wait_ge(const_in, 16 * N_CONST)
            high_turned(lambda k: gmix[:, k:k + 1])

            act.wait_ge(unit_done, 1)
            nc.scalar.activation(alow_t[0:RANK, :], bank[0][0:RANK, :], ACT.Copy).then_inc(evac[0], 1)
            high_part()

            start = AT["v"]
            acc, done = Count(start["acc"]), Count(start["unit"])
            with repeat(act, NB, *units(4), (acc, 3), (done, 4)) as nb:
                for kg in range(4):
                    now = done.next()
                    if kg == 3:
                        for t in range(TT):
                            if t < TT - 1:
                                act.wait_ge(acc_done, acc.next())
                            else:
                                act.wait_ge(unit_done, now)
                            nc.scalar.activation(xa[:, t, bass.ds(nb * BW, BW)], bank[t][:],
                                                 ACT.Gelu).then_inc(evac[t], 1)
                    high_part()
            act.wait_ge(var_done, 1)
            nc.scalar.activation(var_root[:], var[:], ACT.Sqrt).then_inc(var_rooted, 1)

            start = AT["gates"]
            done = Count(start["unit"])
            read = [Count(start["evac"][j]) for j in range(2)]
            stored = [Count(), Count()]

            def gate_unit(j, index, first):
                high_part()
                act.wait_ge(unit_done, done.next())
                if not first:
                    act.wait_ge(gates_out[j], stored[j].now())
                nc.scalar.activation(sgu_act[:, j, :], bank[j][:], ACT.Sigmoid).then_inc(evac[j], 1)
                act.wait_ge(evac[j], read[j].next())
                stored[j].next(16)
                dst = gates_dram[index] if isinstance(index, int) else gates_dram[
                    bass.ds(index, 1)].rearrange("a p n -> (a p) n")
                act.dma_start(dst, sgu_act[:, j, :]).then_inc(gates_out[j], 16)

            for j in range(2):
                gate_unit(j, j, True)
            with repeat(act, KT - 1, *units(2), (done, 2), (read[0], 1), (read[1], 1), (stored[0], 16),
                        (stored[1], 16)) as i:
                for j in range(2):
                    gate_unit(j, i * 2 + (2 + j), False)
            for j in range(2):
                act.wait_ge(gates_out[j], stored[j].now())

            done, used = Count(AT["spatial"]["unit"]), Count()

            def u_unit(j, first):
                high_part()
                act.wait_ge(unit_done, done.next())
                if not first:
                    act.wait_ge(sgu_done, used.next())
                nc.scalar.activation(sgu_act[:, j, :], bank[j][:], ACT.Gelu).then_inc(evac[j], 1)

            for j in range(2):
                u_unit(j, True)
            with repeat(act, KT // 2 - 1, *units(2), (done, 2), (used, 2)):
                for j in range(2):
                    u_unit(j, False)

            act.wait_ge(sgu_done, KT)
            start = AT["attention"]
            done, acc = Count(start["unit"]), Count(start["acc"])
            heads, silu_used, tiles = Count(), Count(-2), Count()
            with repeat(act, HEADS, *units(12), (done, 12), (acc, 6), (heads, 1), (silu_used, TT),
                        (tiles, TT), (step, 3)) as h:
                head = heads.next()
                act.dma_start(wup_stage[0:RANK, :], w_up[:, bass.ds(h * DK, DK)]).then_inc(wup_staged, 16)
                high_part()
                done.next()
                act.wait_ge(z_done, head)
                for dt in range(DT):
                    bias = balpha[:, bass.ds(h * DT + dt, 1)]
                    tmp = k_inv[:, dt, :]
                    then(nc.scalar.activation(tmp, bank[6 + dt][:], ACT.Abs, bias=bias))
                for dt in range(DT):
                    tmp = k_inv[:, dt, :]
                    ins = nc.scalar.activation(tmp, tmp, ACT.Exp, scale=-1.0)
                then(ins)
                for dt in range(DT):
                    tmp = k_inv[:, dt, :]
                    ins = nc.scalar.activation(tmp, tmp, ACT.Ln, bias=1.0)
                ins.then_inc(soft_done, 1)
                high_part()
                done.next()
                act.wait_ge(cum_done, head)
                nc.scalar.activation(q_dec[:], k_end[:], ACT.Exp, scale=1.0 / GATE_TEMP)
                nc.scalar.activation(k_inv[:], k_end[:], ACT.Exp,
                                     scale=-1.0 / GATE_TEMP).then_inc(exps_done, 1)
                high_part()
                done.next()
                now = done.next()
                for t in range(TT):
                    if t < TT - 1:
                        act.wait_ge(acc_done, acc.next())
                    else:
                        act.wait_ge(unit_done, now)
                    nc.scalar.activation(vals[:, t, :], bank[t][:], ACT.Copy).then_inc(evac[t], 1)
                high_part()
                for _ in range(2):
                    done.next()
                    high_part()
                done.next()
                high_part()
                act.wait_ge(ke_turned, head)
                for dt in range(DT):
                    ins = nc.scalar.activation(
                        k_end_t[:, :, dt * P:(dt + 1) * P],
                        bank[4 + dt][:].rearrange("p (t d) -> p t d", d=P), ACT.Copy)
                ins.then_inc(ke_done, 1)
                done.next()
                high_part()

                def o_tile(t):
                    o = bank[5 - t % 2]
                    act.wait_ge(o_mm, tiles.next())
                    nc.scalar.activation(silu_out[:, 0, :], o[:], ACT.Square,
                                         accum_out=head_squares[:, t:t + 1])
                    nc.scalar.activation(xb[:, t, bass.ds(h * DV, DV)], o[:], ACT.Copy).then_inc(o_done, 1)
                    act.wait_ge(o_done, tiles.now())

                done.next()
                high_part()
                o_tile(0)
                o_tile(1)
                done.next()
                high_part()
                o_tile(2)
                done.next()
                high_part()
                now = done.next()

                def silu(t):
                    if t < TT - 1:
                        act.wait_ge(acc_done, acc.next())
                    else:
                        act.wait_ge(unit_done, now)
                    if t >= 2:
                        act.wait_ge(y_done, silu_used.now(t + 1))
                    nc.scalar.activation(silu_out[:, t % 2, :], bank[t][:], ACT.Silu).then_inc(evac[t], 1)

                o_tile(3)
                act.wait_ge(head_ms_done, head)
                nc.scalar.activation(head_root[:], head_ms[:], ACT.Sqrt).then_inc(head_rooted, 1)
                for t in range(TT):
                    silu(t)
                silu_used.next(TT)
                high_part()

            act.wait_ge(sgu_done, KT)
            for k in range(KT):
                nc.scalar.activation(x_high[:, k, :].rearrange("p (t c) -> p t c", c=P),
                                     xa[:, :, k * P:(k + 1) * P], ACT.Copy).then_inc(xh_done, 1)

            def load_gate(index, slot, wait):
                if wait:
                    act.wait_ge(evac[slot], read[slot].next())
                src = gates_dram[index] if isinstance(index, int) else gates_dram[
                    bass.ds(index, 1)].rearrange("a p n -> (a p) n")
                act.dma_start(gate_in[:, slot, :], src).then_inc(gate_loaded[slot], 16)

            act.wait_ge(y_done, HEADS * TT)
            for j in range(2):
                load_gate(j, j, False)
            act.wait_ge(xl_done, 2 * KT)
            act.dma_start(xa[:], x.rearrange("(t p) d -> p t d", p=P)).then_inc(x_again, 16)
            read = [Count(AT["merge_spatial"]["evac"][j]) for j in range(2)]
            with repeat(act, KT // 2, *units(2), (read[0], 1), (read[1], 1)) as i:
                for j in range(2):
                    high_part()
                    load_gate(i * 2 + (2 + j), j, True)

            high_turned(lambda k: normg[:, k % (DV // P):k % (DV // P) + 1])
            with repeat(act, KT // 2 - 1, *units(2), (read[0], 1), (read[1], 1)) as i:
                for j in range(2):
                    high_part()
                    load_gate(i * 2 + (KT + 2 + j), j, True)
            for j in range(2):
                high_part()

            for k in range(KT):
                act.wait_ge(merge_done, k + 1)
                nc.scalar.activation(x_high[:, k, :], merged[:, k, :], ACT.Copy).then_inc(xh_done, 1)
            act.wait_ge(xl_done, 4 * KT)
            act.dma_start(skeys[:], keys_t).then_inc(keys_in, 16)
            with repeat(act, 2 * (NB - 1), *units(2)):
                for j in range(2):
                    high_part()
            for t in range(TT):
                act.wait_ge(evac[t], AT["query"]["evac"][t] - 1)
                square_sum(t, 0, 0, D - BW)
            for _ in range(4):
                high_part()

            for t in range(TT):
                act.wait_ge(evac[t], AT["query"]["evac"][t])
                square_sum(t, 1, D - BW, D)
            act.wait_ge(ms_done, 2)
            nc.scalar.activation(norm_root[:], norm_ms[:], ACT.Sqrt).then_inc(root_done, 1)
            high_turned(lambda k: gffn[:, k:k + 1])

            done, scans, used = Count(AT["query"]["unit"]), Count(), Count()

            def query_head(first):
                for p in range(2):
                    act.wait_ge(unit_done, done.next())
                    nc.scalar.activation(q_t[:, p, :], bank[p][:], ACT.Copy).then_inc(evac[p], 1)
                    high_part()
                for p in range(2):
                    act.wait_ge(scored, scans.next())
                    if not first:
                        act.wait_ge(topped, used.next())
                    nc.scalar.activation(scores[:, p, :], bank[4 + p][:], ACT.Copy).then_inc(scores_done, 1)

            query_head(True)
            with repeat(act, PH - 1, *units(2), (done, 2), (scans, 2), (used, 2)):
                query_head(False)

            start = AT["experts"]
            done = Count(start["unit"])
            read = [Count(start["evac"][j]) for j in range(2)]
            stored = [Count(), Count()]
            steps = Count(1)

            def expert_unit(j, index, first=False):
                high_part()
                act.wait_ge(unit_done, done.next())
                if not first:
                    act.wait_ge(act_stored[j], stored[j].now())
                nc.scalar.activation(act_out[:, j, :], bank[j][:], ACT.Gelu).then_inc(evac[j], 1)
                act.wait_ge(evac[j], read[j].next())
                stored[j].next(16)
                dst = act_dram[index] if isinstance(index, int) else act_dram[
                    bass.ds(index, 1)].rearrange("a p n -> (a p) n")
                act.dma_start(dst, act_out[:, j, :]).then_inc(act_stored[j], 16)

            def experts(n):
                return [*units(n), (done, n), (read[0], n // 2), (read[1], n // 2), (stored[0], 8 * n),
                        (stored[1], 8 * n)]

            def gate_step(j, token):
                act.wait_ge(step_mm, steps.next())
                for half in range(2):
                    where = stage[:, :, bass.ds(token + 4 * half, 4)] if not isinstance(
                        token, int) else stage[:, :, token + 4 * half:token + 4 * half + 4]
                    ins = nc.scalar.activation(
                        where.rearrange("p i t -> p t i"),
                        bank[4 + 2 * j + half][:].rearrange("p (t i) -> p t i", i=P), ACT.Copy)
                ins.then_inc(step_out, 1)

            def pairs(n, index, then_do=None):
                with repeat(act, n, *experts(2)) as i:
                    for j in range(2):
                        expert_unit(j, index + (i * 2 + j))

            for j in range(2):
                expert_unit(j, j, True)
            pairs(2, 2)
            act.wait_ge(peer_diff, 1)
            nc.scalar.activation(all_best[:], all_best[:], ACT.Exp).then_inc(peer_exp, 1)
            pairs((LEAD - 6) // 2, 6)
            act.wait_ge(slots_turned, 1)
            for src, dst in ((4, idx1_t), (5, idx2_t)):
                nc.scalar.activation(dst[:], bank[src][:], ACT.Copy)
            nc.scalar.activation(gate_parts[:, 0, :], bank[6][:], ACT.Copy).then_inc(slot_gate_high, 1)

            kept_stages = Count()

            def stage_units(s, first=False, last=False):
                index = s * STAGE_UNITS + LEAD
                if not first:
                    act.wait_ge(stage_out, kept_stages.now())
                kept_stages.next(16 * PIECES)
                with repeat(act, STAGE_TOK // WTOK // 2, *experts(2), (steps, 2)) as q:
                    for j in range(2):
                        expert_unit(j, index + (q * 2 + j))
                        gate_step(j, q * (2 * WTOK) + j * WTOK)
                act.wait_ge(step_out, steps.now(1))
                index = index + STAGE_TOK // WTOK
                for n in range(STAGE_UNITS - STAGE_TOK // WTOK):
                    if n < PIECES:
                        firsts = slice(n * P // PIECES, (n + 1) * P // PIECES)
                        tokens = slice(s * STAGE_TOK, (s + 1) * STAGE_TOK) if isinstance(
                            s, int) else bass.ds(s * STAGE_TOK, STAGE_TOK)
                        act.dma_start(retrieved_dram[firsts, :, tokens].rearrange("i j t -> j i t"),
                                      stage[:, firsts, :]).then_inc(stage_out, 16)
                    elif last:
                        if n == PIECES:
                            act.wait_ge(stage_out, kept_stages.now())
                        load_pair(n - PIECES, n - PIECES)
                        if n == PIECES + 1:
                            product_high(0)
                    expert_unit(n % 2, index + n)

            def load_pair(group, slot):
                for dram, tile in ((act_dram, act_in), (retrieved_dram, gates_in)):
                    src = dram[group * EG:(group + 1) * EG] if isinstance(group, int) else dram[
                        bass.ds(group * EG, EG)]
                    act.dma_start(tile[:, slot, :, :], src.rearrange("e p t -> p e t")).then_inc(
                        pair_in[slot], 16)

            products, lows = Count(), Count()

            def product_high(slot):
                act.wait_ge(product_done, products.next())
                nc.scalar.activation(a_high[:, slot, :, :], act_in[:, slot, :, :],
                                     ACT.Copy).then_inc(ah_done, 1)

            n_stages = T // STAGE_TOK
            stage_units(0, first=True)
            with repeat(act, n_stages - 2, *experts(STAGE_UNITS), (steps, STAGE_TOK // WTOK),
                        (kept_stages, 16 * PIECES)) as s:
                stage_units(s + 1)
            stage_units(n_stages - 1, last=True)

            def value_group(group, slot, prepare=True, load=True, n_high=4):
                high_part()
                if prepare:
                    product_high(slot ^ 1)
                high_part()
                if n_high > 2:
                    high_part()
                if load:
                    act.wait_ge(al_done, lows.next())
                    load_pair(group + 3, slot ^ 1)
                if n_high > 2:
                    high_part()

            for j in range(2):
                act.wait_ge(act_stored[j], stored[j].now())
            act.wait_ge(al_done, lows.next())
            load_pair(2, 0)
            act.dma_start(gfin[:], g_final.partition_broadcast(P)).then_inc(gfin_in, 16)
            n_groups = ETILES // EG
            with repeat(act, n_groups // 2 - 2, *units(8), (products, 2), (lows, 2)) as i:
                value_group(i * 2, 0)
                value_group(i * 2 + 1, 1)
            value_group(n_groups - 4, 0)
            value_group(n_groups - 3, 1, load=False)
            value_group(n_groups - 2, 0, load=False)
            value_group(n_groups - 1, 1, prepare=False, load=False, n_high=2)

            for t in range(TT):
                act.wait_ge(evac[t], AT["end"]["evac"][t] - 1)
                square_sum(t, 0, 0, D - BW)

            def root(t):
                act.wait_ge(ms_done, 3 + t)
                nc.scalar.activation(norm_root[:, t:t + 1], norm_ms[:, t:t + 1],
                                     ACT.Sqrt).then_inc(root_done, 1)

            for t in range(TT):
                act.wait_ge(evac[t], AT["end"]["evac"][t])
                square_sum(t, 1, D - BW, D)
                if t > 0:
                    root(t - 1)
            root(TT - 1)
            for t in range(TT):
                act.wait_ge(normed, 2 * NB + t + 1)
                act.dma_start(out[t * P:(t + 1) * P, :], xb[:, t, :]).then_inc(out_done, 16)
            act.wait_ge(out_done, 16 * TT)

        @block.vector
        def _(dve):
            step = Count()
            turns, xh = Count(), Count()

            def then(ins):
                ins.then_inc(dve_step, 1)
                dve.wait_ge(dve_step, step.next())

            def norm_rows(k):
                dve.wait_ge(sq_done, 2 * TT * (k + 1))
                then(nc.vector.tensor_tensor(squares_sum[:], squares[:, 0, :], squares[:, 1, :], ALU.add))
                nc.vector.tensor_scalar(norm_ms[:], squares_sum[:], 1.0 / D, EPS, ALU.mult,
                                        ALU.add).then_inc(ms_done, 1)
                dve.wait_ge(root_done, k + 1)
                then(nc.vector.reciprocal(norm_inv[:], norm_root[:]))
                for b in range(NB):
                    cols = slice(b * BW, (b + 1) * BW)
                    for t in range(TT):
                        ins = nc.vector.tensor_scalar(xb[:, t, cols], xa[:, t, cols], norm_inv[:, t:t + 1], None,
                                                      ALU.mult)
                    ins.then_inc(normed, 1)

            def low_turned(gain):
                for k in range(KT):
                    dve.wait_ge(xh_done, xh.next())
                    nc.vector.scalar_tensor_tensor(
                        out=x_low[:, k, :], in0=bank[4 + k % 4][:], scalar=gain(k),
                        in1=x_high[:, k, :].bitcast(F32), op0=ALU.mult, op1=ALU.subtract).then_inc(xl_done, 1)

            norm_rows(0)
            low_turned(lambda k: gmix[:, k:k + 1])

            read = [Count(AT["v"]["evac"][t]) for t in range(TT)]
            with repeat(dve, NB, (step, 1), *[(read[t], 1) for t in range(TT)]) as nb:
                for t in range(TT):
                    dve.wait_ge(evac[t], read[t].next())
                    ins = nc.vector.bn_stats(bn[:, t, bass.ds(nb, 1), :].rearrange("p a s -> p (a s)"),
                                             xa[:, t, bass.ds(nb * BW, BW)])
                then(ins)
            for t in range(TT):
                ins = nc.vector.bn_aggr(mean_var[:, t, :], bn[:, t, :, :].rearrange("p a s -> p (a s)"))
            then(ins)
            nc.vector.tensor_scalar(var[:], mean_var[:, :, 1], EPS, None, ALU.add).then_inc(var_done, 1)
            dve.wait_ge(var_rooted, 1)
            then(nc.vector.reciprocal(var_inv[:], var_root[:]))
            for t in range(TT):
                ins = nc.vector.tensor_scalar(xa[:, t, :], xa[:, t, :], mean_var[:, t, 0:1], var_inv[:, t:t + 1],
                                              ALU.subtract, ALU.mult)
            then(ins)

            read = [Count(AT["spatial"]["evac"][j]) for j in range(2)]
            mixes, products = Count(), Count()
            dve.wait_ge(const_made, 2)

            def over_tokens(ap, n):
                return ap.unsqueeze(1).to_broadcast([P, TT, n])

            with repeat(dve, GROUPS, (mixes, 2), (products, 2), (read[0], 1), (read[1], 1), (step, 3)) as g:
                nc.vector.tensor_copy(ws_stage[:], ws[:, bass.ds(g, 1), :].rearrange("p a t -> p (a t)"))
                then(nc.vector.tensor_tensor(vstage[:], xa[:, :, bass.ds(g * (2 * P), 2 * P)],
                                             over_tokens(lng[:, bass.ds(g * (2 * P), 2 * P)], 2 * P), ALU.mult))
                nc.vector.tensor_tensor(vstage[:], vstage[:],
                                        over_tokens(lnb[:, bass.ds(g * (2 * P), 2 * P)], 2 * P),
                                        ALU.add).then_inc(vstage_done, 1)
                for j in range(2):
                    dve.wait_ge(mixed, mixes.next())
                    then(nc.vector.tensor_tensor(
                        sgu_sum[:].rearrange("p (t c) -> p t c", c=P),
                        bank[4 + j][:].rearrange("p (t c) -> p t c", c=P),
                        bs[:, bass.ds(g, 1), :].to_broadcast([P, TT, P]), ALU.add))
                    dve.wait_ge(evac[j], read[j].next())
                    nc.vector.tensor_tensor(
                        xa[:, :, bass.ds(g * (2 * P) + j * P, P)],
                        sgu_sum[:].rearrange("p (t c) -> p t c", c=P),
                        sgu_act[:, j, :].rearrange("p (t c) -> p t c", c=P), ALU.mult).then_inc(sgu_done, 1)
                    dve.wait_ge(sgu_done, products.next())

            nc.vector.memset(att_t[:], 0.0)
            start = AT["attention"]
            done, heads, states = Count(start["unit"]), Count(), Count()
            read = [Count(start["evac"][t]) for t in range(TT)]
            tiles = Count()
            with repeat(dve, HEADS, (done, 12), (heads, 1), (states, TT - 1), (tiles, TT),
                        *[(read[t], 3) for t in range(TT)], (step, 6)) as h:
                head = heads.next()
                dve.wait_ge(soft_done, head)
                for dt in range(DT):
                    ins = nc.vector.tensor_scalar(q_dec[:, dt, :], bank[6 + dt][:], balpha[:, bass.ds(h * DT + dt, 1)],
                                                  0.0, ALU.add, ALU.min)
                then(ins)
                then(nc.vector.tensor_tensor(q_dec[:], q_dec[:], k_inv[:], ALU.subtract))
                for dt in range(DT):
                    ins = nc.vector.tensor_tensor_scan(k_end[:, dt, :], scan_keep[:], q_dec[:, dt, :], 0.0,
                                                       ALU.mult, ALU.add)
                ins.then_inc(cum_done, 1)
                dve.wait_ge(exps_done, head)
                then(nc.vector.tensor_copy(decay[:], q_dec[:].rearrange(
                    "p d (n c) -> p d n c", c=CHUNK)[:, :, :, CHUNK - 1]))
                in_pairs = [tile[:].rearrange("p d (t b) -> p (d t) b", b=2) for tile in (decay, k_decay, q_decay)]
                nc.vector.memset(q_decay[:], 1.0)
                then(nc.vector.tensor_copy(k_decay[:], decay[:]))
                nc.vector.tensor_tensor(in_pairs[1][:, :, 0], in_pairs[0][:, :, 0], in_pairs[0][:, :, 1], ALU.mult)
                then(nc.vector.tensor_copy(in_pairs[2][:, :, 1], in_pairs[0][:, :, 0]))
                done.next(4)
                for t in range(TT):
                    read[t].next()
                for dt in range(DT):
                    dve.wait_ge(unit_done, done.next())
                    read[dt].next()
                    nc.vector.tensor_tensor(k_inv[:, dt, :], bank[dt][:], k_inv[:, dt, :],
                                            ALU.mult).then_inc(evac[dt], 1)
                    dve.wait_ge(evac[dt], read[dt].now())
                    ins = nc.vector.tensor_tensor(
                        k_end[:, dt, :].rearrange("p (n c) -> p n c", c=CHUNK),
                        k_inv[:, dt, :].rearrange("p (n c) -> p n c", c=CHUNK),
                        k_decay[:, dt, :].unsqueeze(2).to_broadcast([P, NCH, CHUNK]), ALU.mult)
                ins.then_inc(k_done, 1)
                for dt in range(DT):
                    dve.wait_ge(unit_done, done.next())
                    read[2 + dt].next()
                    nc.vector.scalar_tensor_tensor(out=q_dec[:, dt, :], in0=bank[2 + dt][:], scalar=float(DK) ** -0.5,
                                                   in1=q_dec[:, dt, :], op0=ALU.mult,
                                                   op1=ALU.mult).then_inc(evac[2 + dt], 1)
                    dve.wait_ge(evac[2 + dt], read[2 + dt].now())
                    ins = nc.vector.tensor_tensor(
                        q_in[:, dt, :].rearrange("p (n c) -> p n c", c=CHUNK),
                        q_dec[:, dt, :].rearrange("p (n c) -> p n c", c=CHUNK),
                        q_decay[:, dt, :].unsqueeze(2).to_broadcast([P, NCH, CHUNK]), ALU.mult)
                ins.then_inc(q_done, 1)
                dve.wait_ge(att_done, head)
                nc.vector.memset(wait_at[:], 0.0)
                nc.vector.copy_predicated(att_t[:], att_keep[:].bitcast(U32).unsqueeze(1).to_broadcast([P, TT, P]),
                                          bank[4][:].rearrange("p (t c) -> p t c", c=P)).then_inc(att_kept, 1)
                for n in range(TT - 1):
                    dve.wait_ge(state_mm, states.next())
                    for dt in range(DT):
                        if n == 0:
                            ins = nc.vector.tensor_copy(state[:, dt, :], bank[6 + dt][:])
                        else:
                            ins = nc.vector.scalar_tensor_tensor(
                                out=state[:, dt, :], in0=state[:, dt, :], scalar=k_decay[:, dt, 2 * n:2 * n + 1],
                                in1=bank[6 + dt][:], op0=ALU.mult, op1=ALU.add)
                    ins.then_inc(state_done, 1)
                done.next(4)
                dve.wait_ge(o_done, tiles.now(TT))
                nc.vector.tensor_scalar(head_ms[:], head_squares[:], 1.0 / DV, EPS, ALU.mult,
                                        ALU.add).then_inc(head_ms_done, 1)
                dve.wait_ge(head_rooted, head)
                then(nc.vector.reciprocal(head_inv[:], head_root[:]))
                for t in range(TT):
                    tiles.next()
                    dve.wait_ge(evac[t], read[t].next())
                    nc.vector.scalar_tensor_tensor(
                        out=xb[:, t, bass.ds(h * DV, DV)], in0=xb[:, t, bass.ds(h * DV, DV)],
                        scalar=head_inv[:, t:t + 1], in1=silu_out[:, t % 2, :], op0=ALU.mult,
                        op1=ALU.mult).then_inc(y_done, 1)

            for k in range(KT):
                dve.wait_ge(xh_done, xh.next())
                nc.vector.tensor_tensor(x_low[:, k, :].rearrange("p (t c) -> p t c", c=P),
                                        xa[:, :, k * P:(k + 1) * P],
                                        x_high[:, k, :].bitcast(F32).rearrange("p (t c) -> p t c", c=P),
                                        ALU.subtract).then_inc(xl_done, 1)
            done = Count(AT["merge_spatial"]["unit"])
            loads = [Count(), Count()]
            with repeat(dve, KT // 2, (done, 2), (loads[0], 16), (loads[1], 16)) as i:
                for j in range(2):
                    dve.wait_ge(unit_done, done.next())
                    dve.wait_ge(gate_loaded[j], loads[j].next(16))
                    nc.vector.tensor_tensor(merged[:, bass.ds(i * 2 + j, 1), :].rearrange("p a t -> p (a t)"),
                                            bank[j][:], gate_in[:, j, :], ALU.mult).then_inc(evac[j], 1)

            low_turned(lambda k: normg[:, k % (DV // P):k % (DV // P) + 1])
            read = [Count(AT["merge_attention"]["evac"][j]) for j in range(2)]
            merges = Count()
            with repeat(dve, KT // 2, (merges, 2), (done, 2), (loads[0], 16), (loads[1], 16), (read[0], 1),
                        (read[1], 1)) as i:
                for j in range(2):
                    dve.wait_ge(unit_done, done.next())
                    dve.wait_ge(gate_loaded[j], loads[j].next(16))
                    nc.vector.tensor_tensor(gate_mul[:], bank[j][:], gate_in[:, j, :],
                                            ALU.mult).then_inc(evac[j], 1)
                    dve.wait_ge(evac[j], read[j].next())
                    tile = merged[:, bass.ds(i * 2 + j, 1), :].rearrange("p a t -> p (a t)")
                    nc.vector.tensor_tensor(tile, tile, gate_mul[:], ALU.add).then_inc(merge_done, 1)
                    dve.wait_ge(merge_done, merges.next())

            for k in range(KT):
                dve.wait_ge(xh_done, xh.next())
                nc.vector.tensor_tensor(x_low[:, k, :], merged[:, k, :], x_high[:, k, :].bitcast(F32),
                                        ALU.subtract).then_inc(xl_done, 1)
            start = AT["residual"]
            done, acc = Count(start["unit"]), Count(start["acc"])
            dve.wait_ge(x_again, 16)
            with repeat(dve, NB, (done, 4), (acc, 3)) as nb:
                for t in range(TT):
                    if t < TT - 1:
                        dve.wait_ge(acc_done, acc.next())
                    else:
                        dve.wait_ge(unit_done, done.next(4))
                    where = xa[:, t, bass.ds(nb * BW, BW)]
                    nc.vector.tensor_tensor(where, bank[t][:], where, ALU.add).then_inc(evac[t], 1)

            norm_rows(1)
            low_turned(lambda k: gffn[:, k:k + 1])

            scans = Count()

            def take_wait():
                nc.vector.memset(wait_at[:], 0.0)

            def top16(values, masked_values, out_v, out_i, last_sem=None):
                take_wait()
                for t in range(TT):
                    ins = nc.vector.max(out_v(t)[:, 0:8], values(t))
                then(ins)
                take_wait()
                for t in range(TT):
                    nc.vector.max_index(out_i(t)[:, 0:8], out_v(t)[:, 0:8], values(t))
                    ins = nc.vector.match_replace(masked_values(t), out_v(t)[:, 0:8], values(t), LOWEST)
                then(ins)
                take_wait()
                for t in range(TT):
                    ins = nc.vector.max(out_v(t)[:, 8:16], masked_values(t))
                then(ins)
                take_wait()
                for t in range(TT):
                    ins = nc.vector.max_index(out_i(t)[:, 8:16], out_v(t)[:, 8:16], masked_values(t))
                return ins

            with repeat(dve, PH, (scans, 2), (step, 13)) as h:
                for p in range(2):
                    dve.wait_ge(scores_done, scans.next())
                    then(top16(lambda t: scores[:, p, t * P:(t + 1) * P], lambda t: masked[:, t, :],
                               lambda t: top_v[:, t, p, :], lambda t: top_i[:, t, p, :]))
                    nc.vector.tensor_copy(
                        all_i[:, :, p, bass.ds(h, 1), :].rearrange("p t a k -> p t (a k)"),
                        top_i[:, :, p, :]).then_inc(topped, 1)
                for t in range(TT):
                    ins = nc.vector.tensor_tensor(
                        cand[:, t, :].rearrange("p (a b) -> p a b", b=TOPK),
                        top_v[:, t, 0, :].unsqueeze(2).to_broadcast([P, TOPK, TOPK]),
                        top_v[:, t, 1, :].unsqueeze(1).to_broadcast([P, TOPK, TOPK]), ALU.add)
                then(ins)
                then(top16(lambda t: cand[:, t, :], lambda t: cand_masked[:, t, :],
                           lambda t: best[:, t, :], lambda t: pos[:, t, :]))
                nc.vector.tensor_copy(all_best[:, :, bass.ds(h, 1), :].rearrange("p t a k -> p t (a k)"), best[:])
                nc.vector.tensor_copy(all_pos[:, :, bass.ds(h, 1), :].rearrange("p t a k -> p t (a k)"), pos[:])

            then(nc.vector.memset(peer_sum[:], 0.0))
            best_v = all_best[:].rearrange("p t h k -> p (t h) k")
            nc.vector.tensor_copy(peer_sum[:, 0, :], best_v[:, :, 0])
            then(nc.vector.tensor_copy(peer_sum[:, 1, :], best_v[:, :, 0]))
            nc.vector.tensor_tensor(best_v, best_v,
                                    peer_sum[:, 0, :].unsqueeze(2).to_broadcast([P, TT * PH, TOPK]),
                                    ALU.subtract).then_inc(peer_diff, 1)
            pos_v = all_pos[:].rearrange("p t h k -> p t (h k)")
            nc.vector.tensor_single_scalar(pos_half[:, 0, :, :], pos_v, 4, ALU.logical_shift_right)
            then(nc.vector.tensor_single_scalar(pos_half[:, 1, :, :], pos_v, TOPK - 1, ALU.bitwise_and))
            then(nc.vector.tensor_copy(pos_f[:], pos_half[:]))
            for t in range(TT):
                for p in range(2):
                    then(nc.vector.tensor_tensor(onehot16[:], iota16[:].unsqueeze(1).to_broadcast([P, P, TOPK]),
                                                 pos_f[:, p, t, :].unsqueeze(2).to_broadcast([P, P, TOPK]),
                                                 ALU.is_equal))
                    then(nc.vector.tensor_tensor(
                        picked[:].rearrange("p (h k) a -> p h k a", k=TOPK),
                        onehot16[:].rearrange("p (h k) a -> p h k a", k=TOPK),
                        all_i[:, t, p, :, :].unsqueeze(2).to_broadcast([P, PH, TOPK, TOPK]), ALU.mult))
                    then(nc.vector.tensor_reduce(expert_i[:, p, t, :], picked[:], AX_X, ALU.add))
            dve.wait_ge(peer_exp, 1)
            then(nc.vector.tensor_reduce(peer_sum[:, 0, :], best_v, AX_X, ALU.add))
            then(nc.vector.reciprocal(peer_sum[:, 1, :], peer_sum[:, 0, :]))
            nc.vector.tensor_tensor(best_v, best_v,
                                    peer_sum[:, 1, :].unsqueeze(2).to_broadcast([P, TT * PH, TOPK]),
                                    ALU.mult).then_inc(slots_done, 1)

            dve.wait_ge(slot_gate_high, 1)
            then(nc.vector.tensor_tensor(gate_rest[:], bank[6][:], gate_parts[:, 0, :], ALU.subtract))
            then(nc.vector.tensor_copy(gate_parts[:, 1, :], gate_rest[:]))
            then(nc.vector.tensor_tensor(gate_rest2[:], gate_rest[:], gate_parts[:, 1, :], ALU.subtract))
            then(nc.vector.tensor_copy(gate_parts[:, 2, :], gate_rest2[:]))
            steps = Count()

            def by_key(tile, token):
                return tile[:, bass.ds(token, WTOK)].unsqueeze(2).to_broadcast([P, WTOK, P])

            keys = iota[:].unsqueeze(1).to_broadcast([P, WTOK, P])
            with repeat(dve, T // WTOK, (steps, 1), (step, 1)) as s:
                token = s * WTOK
                dve.wait_ge(step_mm, steps.next())
                then(nc.vector.tensor_tensor(hit1[:], keys, by_key(idx1_t, token), ALU.is_equal))
                for part in range(3):
                    nc.vector.tensor_tensor(rows[:, part, :, :], hit1[:], by_key(gate_parts[:, part, :], token),
                                            ALU.mult)
                nc.vector.tensor_tensor(hit2[:], keys, by_key(idx2_t, token),
                                        ALU.is_equal).then_inc(rows_done, 1)

            pairs = [Count(), Count()]
            highs = Count()

            def product(slot):
                dve.wait_ge(pair_in[slot], pairs[slot].next(32))
                nc.vector.tensor_tensor(act_in[:, slot, :, :], act_in[:, slot, :, :], gates_in[:, slot, :, :],
                                        ALU.mult).then_inc(product_done, 1)

            def product_low(slot):
                dve.wait_ge(ah_done, highs.next())
                nc.vector.tensor_tensor(a_low[:, slot, :, :], act_in[:, slot, :, :],
                                        a_high[:, slot, :, :].bitcast(F32), ALU.subtract).then_inc(al_done, 1)

            start = AT["values"]
            done, acc = Count(start["unit"]), Count(start["acc"])

            def value_group(slot, prepare=True):
                for db in range(NB):
                    for t in range(TT):
                        if t < TT - 1:
                            dve.wait_ge(acc_done, acc.next())
                        else:
                            dve.wait_ge(unit_done, done.next())
                        where = xa[:, t, db * BW:(db + 1) * BW]
                        nc.vector.tensor_tensor(where, bank[t][:], where, ALU.add).then_inc(evac[t], 1)
                        if prepare and (db, t) == (0, 1):
                            product(slot ^ 1)
                        if prepare and (db, t) == (1, 1):
                            product_low(slot ^ 1)

            product(0)
            product_low(0)
            with repeat(dve, ETILES // EG // 2 - 1, (done, 2 * NB), (acc, 6 * NB), (pairs[0], 32),
                        (pairs[1], 32), (highs, 2)):
                value_group(0)
                value_group(1)
            value_group(0)
            value_group(1, prepare=False)

            dve.wait_ge(gfin_in, 16)
            for t in range(TT):
                dve.wait_ge(sq_done, 5 * TT + t + 1)
                then(nc.vector.tensor_tensor(squares_sum[:, t:t + 1], squares[:, 0, t:t + 1],
                                             squares[:, 1, t:t + 1], ALU.add))
                nc.vector.tensor_scalar(norm_ms[:, t:t + 1], squares_sum[:, t:t + 1], 1.0 / D, EPS, ALU.mult,
                                        ALU.add).then_inc(ms_done, 1)
                dve.wait_ge(root_done, 3 + t)
                then(nc.vector.reciprocal(norm_inv[:, t:t + 1], norm_root[:, t:t + 1]))
                nc.vector.scalar_tensor_tensor(out=xb[:, t, :], in0=xa[:, t, :], scalar=norm_inv[:, t:t + 1],
                                               in1=gfin[:], op0=ALU.mult, op1=ALU.mult).then_inc(normed, 1)

        @block.tensor
        def _(pe):
            unit, slot = Count(), 0
            free = [Count() for _ in range(4)]
            filled = Count()

            def weights_ready():
                pe.wait_ge(low_done, unit.next())

            def column(b, tile_waits=None):
                nonlocal slot
                weights_ready()
                pe.wait_ge(evac[b], free[b].next())
                for k in range(KT):
                    if tile_waits is not None:
                        pe.wait_ge(xl_done, tile_waits * KT + k + 1)
                    w = slice(k * P, (k + 1) * P)
                    nc.tensor.matmul(bank[b][:], high[:, slot, w], x_high[:, k, :], start=(k == 0), stop=False)
                    nc.tensor.matmul(bank[b][:], high[:, slot, w], x_low[:, k, :], start=False, stop=False)
                    ins = nc.tensor.matmul(bank[b][:], low[:, slot, w], x_high[:, k, :], start=False,
                                           stop=(k == KT - 1))
                ins.then_inc(unit_done, 1)
                slot ^= 1

            def block_unit(kg, refill=None, pause=lambda n: None):
                nonlocal slot
                weights_ready()
                n = 0
                for t in range(TT):
                    if kg == 0:
                        pe.wait_ge(evac[t], free[t].next())
                    for kk in range(4):
                        k = 4 * kg + kk
                        if refill is not None and t == 0:
                            pe.wait_ge(xl_done, refill * KT + k + 1)
                        x_t, w = slice(t * P, (t + 1) * P), slice(kk * BW, (kk + 1) * BW)
                        for left, right, first, last in ((x_high, high, k == 0, False), (x_high, low, False, False),
                                                         (x_low, high, False, k == KT - 1)):
                            ins = nc.tensor.matmul(bank[t][:], left[:, k, x_t], right[:, slot, w], start=first,
                                                   stop=last)
                            if last and t < TT - 1:
                                ins.then_inc(acc_done, 1)
                            if kk == 3 and t == TT - 1 and left is x_low:
                                ins.then_inc(unit_done, 1)
                            n += 1
                            if n % 16 == 0:
                                pause(n // 16 - 1)
                slot ^= 1

            def banks(n):
                return [(free[b], n) for b in range(4)]

            refills = Count()

            def turn(src, blocks_before=None):
                base = refills.now()
                for k in range(KT):
                    if blocks_before is not None and k % (BW // P) == 0:
                        pe.wait_ge(normed, blocks_before + k // (BW // P) + 1)
                    if k >= 4:
                        pe.wait_ge(xl_done, base + k - 3)
                    for t in range(TT):
                        ins = nc.tensor.transpose(bank[4 + k % 4][:, t * P:(t + 1) * P],
                                                  src[:, t, k * P:(k + 1) * P], ident[:])
                    ins.then_inc(turned, 1)

            pe.sem_inc(step_mm, 1)
            pe.wait_ge(const_made, 1)
            turn(xb, blocks_before=0)
            column(0, tile_waits=0)

            with repeat(pe, NB, (unit, 4), *banks(1)):
                for kg in range(4):
                    block_unit(kg)

            with repeat(pe, KT, (unit, 2), (free[0], 1), (free[1], 1)):
                column(0)
                column(1)

            groups, mixes = Count(), Count()

            def u_group(first):
                group = groups.next()
                for j in range(2):
                    column(j)
                    if j == 0:
                        pe.wait_ge(vstage_done, group)
                    if not first:
                        pe.wait_ge(sgu_done, mixes.next())
                    for t in range(TT):
                        ins = nc.tensor.matmul(bank[4 + j][:, t * P:(t + 1) * P], vstage[:, t, j * P:(j + 1) * P],
                                               ws_stage[:], start=True, stop=True)
                    ins.then_inc(mixed, 1)

            u_group(True)
            with repeat(pe, GROUPS - 1, (unit, 2), (free[0], 1), (free[1], 1), (groups, 1), (mixes, 2)):
                u_group(False)

            heads, states, o_tiles, stages = Count(), Count(), Count(), Count()
            with repeat(pe, HEADS, (unit, 12), *banks(3), (heads, 1), (states, TT - 1), (o_tiles, TT),
                        (stages, 16)):
                head = heads.next()
                block_unit(0)
                pe.wait_ge(wup_staged, stages.next(16))
                for dt in range(DT):
                    ins = nc.tensor.matmul(bank[6 + dt][:], wup_stage[0:RANK, dt * P:(dt + 1) * P],
                                           alow_t[0:RANK, :], start=True, stop=True)
                ins.then_inc(z_done, 1)
                for kg in range(1, 4):
                    block_unit(kg)
                column(0)
                column(1)
                column(2)
                pe.wait_ge(k_done, head)
                for dt in range(DT):
                    for t in range(TT):
                        ins = nc.tensor.transpose(bank[4 + dt][:, t * P:(t + 1) * P],
                                                  k_end[:, dt, t * P:(t + 1) * P], ident[:])
                ins.then_inc(ke_turned, 1)
                column(3)

                def pair_scores():
                    pe.wait_ge(ke_done, head)
                    pe.wait_ge(q_done, head)
                    for t in range(TT):
                        first = slice(t * P, t * P + CHUNK)
                        second = slice(t * P + CHUNK, (t + 1) * P)
                        for dt in range(DT):
                            nc.tensor.matmul(bank[4][0:CHUNK, t * P:(t + 1) * P], k_inv[:, dt, first],
                                             q_in[:, dt, t * P:(t + 1) * P], start=(dt == 0), stop=(dt == DT - 1))
                        for dt in range(DT):
                            ins = nc.tensor.matmul(bank[4][CHUNK:P, t * P + CHUNK:(t + 1) * P], k_inv[:, dt, second],
                                                   q_dec[:, dt, second], start=(dt == 0), stop=(dt == DT - 1))
                    ins.then_inc(att_done, 1)

                def pair_output(t):
                    o = bank[5 - t % 2]
                    if t == 0:
                        pe.wait_ge(att_kept, head)
                    if t >= 2:
                        pe.wait_ge(o_done, o_tiles.now(-1))
                    o_tiles.next()
                    ins = nc.tensor.matmul(o[:], att_t[:, t, :], vals[:, t, :], start=True, stop=(t == 0))
                    if t > 0:
                        pe.wait_ge(state_done, states.now())
                        for dt in range(DT):
                            ins = nc.tensor.matmul(o[:], q_in[:, dt, t * P:(t + 1) * P], state[:, dt, :],
                                                   start=False, stop=(dt == DT - 1))
                    ins.then_inc(o_mm, 1)

                def pair_state(t):
                    states.next()
                    for dt in range(DT):
                        ins = nc.tensor.matmul(bank[6 + dt][:], k_end_t[:, t, dt * P:(dt + 1) * P], vals[:, t, :],
                                               start=True, stop=True)
                    ins.then_inc(state_mm, 1)

                def pause(place):
                    if place == 0:
                        pair_scores()
                    elif place in (2, 4, 6, 8):
                        t = place // 2 - 1
                        pair_output(t)
                        if t < TT - 1:
                            pair_state(t)

                for kg in range(4):
                    block_unit(kg, pause=lambda n: pause(3 * kg + n))

            column_pair = [(unit, 2), (free[0], 1), (free[1], 1)]
            column(0, tile_waits=1)
            column(1)
            with repeat(pe, KT // 2 - 1, *column_pair):
                column(0)
                column(1)
            refills = Count(2 * KT)
            pe.wait_ge(y_done, HEADS * TT)
            turn(xb)
            column(0, tile_waits=2)
            column(1)
            with repeat(pe, KT // 2 - 1, *column_pair):
                column(0)
                column(1)

            for kg in range(4):
                block_unit(kg, refill=3)
            with repeat(pe, NB - 1, (unit, 4), *banks(1)):
                for kg in range(4):
                    block_unit(kg)

            refills = Count(4 * KT)
            turn(xb, blocks_before=NB)
            scans = Count()
            pe.wait_ge(keys_in, 16)

            def query_head(h, first):
                column(0, tile_waits=4 if first else None)
                column(1)
                for p in range(2):
                    pe.wait_ge(evac[p], free[p].now(1))
                    if not first:
                        pe.wait_ge(scores_done, scans.next())
                    for t in range(TT):
                        k = skeys[:, p, :] if first else skeys[:, bass.ds(h * 2 + p, 1), :].rearrange(
                            "p a k -> p (a k)")
                        ins = nc.tensor.matmul(bank[4 + p][:, t * P:(t + 1) * P], q_t[:, p, t * P:(t + 1) * P], k,
                                               start=True, stop=True)
                    ins.then_inc(scored, 1)

            query_head(0, True)
            with repeat(pe, PH - 1, *column_pair, (scans, 2)) as h:
                query_head(h + 1, False)

            with repeat(pe, LEAD // 2, *column_pair):
                column(0)
                column(1)
            pe.wait_ge(scores_done, 2 * PH)
            pe.wait_ge(slots_done, 1)
            for b, slots in ((4, expert_i[:, 0, :, :]), (5, expert_i[:, 1, :, :]),
                             (6, all_best[:].rearrange("p t h k -> p t (h k)"))):
                for t in range(TT):
                    ins = nc.tensor.transpose(bank[b][:, t * P:(t + 1) * P], slots[:, t, :], ident[:])
            ins.then_inc(slots_turned, 1)
            made, outs = Count(), Count()

            def gate_step(j):
                pe.wait_ge(rows_done, made.next())
                pe.wait_ge(step_out, outs.next())
                for token in range(WTOK):
                    b, col = 4 + 2 * j + token // 4, token % 4 * P
                    for part in range(3):
                        ins = nc.tensor.matmul(bank[b][:, col:col + P], hit2[:, token, :],
                                               rows[:, part, token, :], start=(part == 0), stop=(part == 2))
                ins.then_inc(step_mm, 1)

            spt = STAGE_TOK // WTOK
            with repeat(pe, T // STAGE_TOK, (unit, STAGE_UNITS), (free[0], STAGE_UNITS // 2),
                        (free[1], STAGE_UNITS // 2), (made, spt), (outs, spt)):
                with repeat(pe, spt // 2, *column_pair, (made, 2), (outs, 2)):
                    for j in range(2):
                        column(j)
                        gate_step(j)
                with repeat(pe, (STAGE_UNITS - spt) // 2, *column_pair):
                    column(0)
                    column(1)

            lows = Count()
            with repeat(pe, ETILES // EG // 2, (unit, 2 * NB), *banks(2 * NB), (lows, 2)):
                for g in range(2):
                    pe.wait_ge(al_done, lows.next())
                    for db in range(NB):
                        weights_ready()
                        for t in range(TT):
                            pe.wait_ge(evac[t], free[t].next())
                            for e in range(EG):
                                a_t, w = slice(t * P, (t + 1) * P), slice(e * BW, (e + 1) * BW)
                                nc.tensor.matmul(bank[t][:], a_high[:, g, e, a_t], high[:, slot, w],
                                                 start=(e == 0), stop=False)
                                nc.tensor.matmul(bank[t][:], a_high[:, g, e, a_t], low[:, slot, w],
                                                 start=False, stop=False)
                                ins = nc.tensor.matmul(bank[t][:], a_low[:, g, e, a_t], high[:, slot, w],
                                                       start=False, stop=(e == EG - 1))
                            ins.then_inc(acc_done if t < TT - 1 else unit_done, 1)
                        slot ^= 1


_CONSTS = ("g_mix", "g_ffn", "g_final", "w_s_t", "b_s", "ln_g", "ln_b", "w_up", "b_alpha", "norm_g", "keys_t")


def kernel(**inputs):
    import numpy as np
    import concourse.bacc as bacc
    from concourse.bass_utils import run_bass_kernel_spmd

    a = {name: np.asarray(value) for name, value in inputs.items()}

    def columns(w):
        return w.reshape(KT, P, -1, P).transpose(2, 1, 0, 3).reshape(-1, P, D)

    def blocks(w):
        return w.reshape(KT // 4, 4, P, -1, BW).transpose(3, 0, 2, 1, 4).reshape(-1, P, D)

    w_in = a["w_in"][0]
    edges = {}
    at = 0
    for name, n in (("u", D), ("v", D), ("q", HEADS * DK), ("k", HEADS * DK), ("vals", HEADS * DV),
                    ("r", HEADS * DV), ("alow", RANK), ("gate_a", D), ("gate_b", D)):
        edges[name] = at
        at += n

    def part(name, start, n):
        return w_in[:, edges[name] + start:edges[name] + start + n]

    stream = [columns(part("alow", 0, P)), blocks(part("v", 0, D)), columns(part("gate_a", 0, 2 * D)),
              columns(part("u", 0, D))]
    for h in range(HEADS):
        stream += [blocks(part("vals", h * DV, DV)), columns(part("k", h * DK, DK)),
                   columns(part("q", h * DK, DK)), blocks(part("r", h * DV, DV))]
    stream += [columns(a["w_branch_a"][0]), columns(a["w_branch_b"][0]), blocks(a["w_out"][0]),
               columns(a["w_query"][0])]
    stream.append(a["expert_u"][0].reshape(ETILES, P, KT, P).transpose(0, 3, 2, 1).reshape(ETILES, P, D))
    stream.append(a["expert_v"][0].reshape(ETILES // EG, EG, P, NB, BW).transpose(0, 3, 2, 1, 4).reshape(
        ETILES, P, D))
    arrays = {
        "x": a["x"][0],
        "weights": np.concatenate(stream),
        "g_mix": a["g_mix"][0].reshape(KT, P).T,
        "g_ffn": a["g_ffn"][0].reshape(KT, P).T,
        "g_final": a["g_final"],
        "w_s_t": a["w_s"][0].transpose(2, 0, 1),
        "b_s": a["b_s"][0].reshape(-1),
        "ln_g": a["ln_v_g"][0],
        "ln_b": a["ln_v_b"][0],
        "w_up": a["w_alpha_up"][0],
        "b_alpha": a["b_alpha"][0].reshape(HEADS * DT, P).T,
        "norm_g": a["gla_norm_g"][0].reshape(DV // P, P).T,
        "keys_t": a["sub_keys"][0].reshape(2 * PH, KEYS, P).transpose(2, 0, 1),
    }
    arrays = {name: np.ascontiguousarray(value) for name, value in arrays.items()}
    nc = bacc.Bacc("TRN2", target_bir_lowering=False, num_devices=1, dynamic_dma_scratch_size=64)
    ins = {name: nc.dram_tensor(name, value.shape, mybir.dt.from_np(value.dtype), kind="ExternalInput").ap()
           for name, value in arrays.items()}
    out = nc.dram_tensor("out", (T, D), F32, kind="ExternalOutput").ap()
    program(nc, ins["x"], ins["weights"], *[ins[name] for name in _CONSTS], out)
    result = run_bass_kernel_spmd(nc, [arrays], core_ids=[0])
    return result.results[0]["out"].reshape(1, T, D)
```
